# Optimizing a Trainium2 kernel written in Bass

```python
import math
import jax, jax.numpy as jnp
from jax import lax
import numpy as np

D_MODEL = 2048
BATCH = 1
SEQ = 256
DEPTH = 1

HEAD_DIM = 128
D_MIX = D_MODEL
GLA_HEADS = D_MIX // 2 // HEAD_DIM
GLA_DK = HEAD_DIM // 2
GLA_DV = HEAD_DIM
GLA_RANK = 16
GLA_TAU = 16.0
GLA_CHUNK = 64
FOX_HEADS = D_MIX // 4 // HEAD_DIM
FOX_BLOCK = 128
MEM_HEADS = 4
MEM_TOKENS = 256
N_OUT_HEADS = GLA_HEADS + FOX_HEADS + MEM_HEADS
D_FF = 4 * D_MODEL
EPS = 1e-6


def _in_widths():
    return (
        GLA_HEADS * GLA_DK,
        GLA_HEADS * GLA_DK,
        GLA_HEADS * GLA_DV,
        GLA_HEADS * GLA_DV,
        GLA_RANK,
        FOX_HEADS * HEAD_DIM,
        FOX_HEADS * HEAD_DIM,
        FOX_HEADS * HEAD_DIM,
        FOX_HEADS * HEAD_DIM,
        FOX_HEADS,
        MEM_HEADS * HEAD_DIM,
        MEM_HEADS * HEAD_DIM,
    )

def _split_points():
    pts, acc = [], 0
    for w in _in_widths()[:-1]:
        acc += w
        pts.append(acc)
    return pts

def rms_norm(x, g):
    xf = x.astype(jnp.float32)
    y = xf * lax.rsqrt(jnp.mean(xf * xf, axis=-1, keepdims=True) + EPS)
    return (y * g.astype(jnp.float32)).astype(x.dtype)

def _heads(t, h):
    return t.reshape(t.shape[0], t.shape[1], h, -1).transpose(0, 2, 1, 3)

def gla_chunked(q, k, v, log_a):
    B, H, S, DK = q.shape
    DV = v.shape[-1]
    C = GLA_CHUNK
    n = S // C

    def to_chunks(t):
        return t.reshape(B, H, n, C, t.shape[-1]).transpose(2, 0, 1, 3, 4)

    qc = to_chunks(q * (DK ** -0.5))
    kc, vc, gc = to_chunks(k), to_chunks(v), to_chunks(log_a)
    causal = jnp.tril(jnp.ones((C, C), dtype=bool))[:, :, None]

    def step(state, xs):
        qi, ki, vi, gi = xs
        b = jnp.cumsum(gi.astype(jnp.float32), axis=2)
        inter = jnp.einsum('bhck,bhkv->bhcv', qi * jnp.exp(b), state)
        rel = b[:, :, :, None, :] - b[:, :, None, :, :]
        decay = jnp.exp(jnp.where(causal, rel, -jnp.inf))
        scores = jnp.einsum('bhik,bhijk,bhjk->bhij', qi.astype(jnp.float32), decay,
                            ki.astype(jnp.float32))
        intra = jnp.einsum('bhij,bhjv->bhiv', scores, vi.astype(jnp.float32))
        b_last = b[:, :, -1:, :]
        new_state = (jnp.exp(b_last[:, :, 0, :])[..., None] * state
                     + jnp.einsum('bhck,bhcv->bhkv', ki * jnp.exp(b_last - b),
                                  vi.astype(jnp.float32)))
        return new_state, inter + intra

    state0 = jnp.zeros((B, H, DK, DV), jnp.float32)
    _, out = lax.scan(step, state0, (qc, kc, vc, gc))
    return out.transpose(1, 2, 0, 3, 4).reshape(B, H, S, DV)

def forgetting_attention(q, k, v, log_f):
    B, H, S, D = q.shape
    scale = D ** -0.5
    c = jnp.cumsum(log_f.astype(jnp.float32), axis=-1)
    outs = []
    for i in range(S // FOX_BLOCK):
        q0, q1 = i * FOX_BLOCK, (i + 1) * FOX_BLOCK
        qb, kb, vb = q[:, :, q0:q1], k[:, :, :q1], v[:, :, :q1]
        logits = (jnp.einsum('bhqd,bhkd->bhqk', qb, kb).astype(jnp.float32) * scale
                  + c[:, :, q0:q1, None] - c[:, :, None, :q1])
        mask = (q0 + jnp.arange(FOX_BLOCK))[:, None] >= jnp.arange(q1)[None, :]
        p = jax.nn.softmax(jnp.where(mask, logits, -jnp.inf), axis=-1)
        outs.append(jnp.einsum('bhqk,bhkd->bhqd', p.astype(v.dtype), vb))
    return jnp.concatenate(outs, axis=2)

def first_inputs(seed: int = 0) -> dict:
    key = jax.random.key(seed)
    ks = jax.random.split(key, 20)
    n = jax.random.normal
    d_in = sum(_in_widths())
    return {
        "x": n(ks[0], (BATCH, SEQ, D_MODEL), jnp.float32),
        "mem": n(ks[1], (BATCH, MEM_TOKENS, D_MODEL), jnp.float32),
        "attn_norm_g": 1.0 + 0.02 * n(ks[2], (D_MODEL,), jnp.float32),
        "w_in": n(ks[3], (D_MODEL, d_in), jnp.float32) * D_MODEL ** -0.5,
        "gla_a_w2": n(ks[4], (GLA_RANK, GLA_HEADS * GLA_DK), jnp.float32) * GLA_RANK ** -0.5,
        "gla_a_b": 0.5 * n(ks[5], (GLA_HEADS * GLA_DK,), jnp.float32),
        "fox_f_b": 3.0 + 0.5 * n(ks[6], (FOX_HEADS,), jnp.float32),
        "fox_q_norm_g": 1.0 + 0.02 * n(ks[7], (HEAD_DIM,), jnp.float32),
        "fox_k_norm_g": 1.0 + 0.02 * n(ks[8], (HEAD_DIM,), jnp.float32),
        "mem_norm_g": 1.0 + 0.02 * n(ks[9], (D_MODEL,), jnp.float32),
        "w_mem_kv": n(ks[10], (D_MODEL, 2 * MEM_HEADS * HEAD_DIM), jnp.float32) * D_MODEL ** -0.5,
        "mem_q_norm_g": 1.0 + 0.02 * n(ks[11], (HEAD_DIM,), jnp.float32),
        "mem_k_norm_g": 1.0 + 0.02 * n(ks[12], (HEAD_DIM,), jnp.float32),
        "out_norm_g": 1.0 + 0.02 * n(ks[13], (N_OUT_HEADS * HEAD_DIM,), jnp.float32),
        "w_out": n(ks[14], (N_OUT_HEADS * HEAD_DIM, D_MODEL), jnp.float32) * (N_OUT_HEADS * HEAD_DIM) ** -0.5,
        "mlp_norm_g": 1.0 + 0.02 * n(ks[15], (D_MODEL,), jnp.float32),
        "w_up": n(ks[16], (D_MODEL, D_FF), jnp.float32) * D_MODEL ** -0.5,
        "w_down": n(ks[17], (D_FF, D_MODEL), jnp.float32) * D_FF ** -0.5,
    }

def first_block(x, mem, attn_norm_g, w_in, gla_a_w2, gla_a_b, fox_f_b, fox_q_norm_g,
              fox_k_norm_g, mem_norm_g, w_mem_kv, mem_q_norm_g, mem_k_norm_g,
              out_norm_g, w_out, mlp_norm_g, w_up, w_down):
    B, S, _ = x.shape
    h = x
    for _layer in range(DEPTH):
        xn = rms_norm(h, attn_norm_g)
        proj = xn @ w_in
        (gq, gk, gv, gg, ga, fq, fk, fv, fg, ff, mq, mg) = jnp.split(proj, _split_points(), axis=-1)

        log_a = jax.nn.log_sigmoid((ga @ gla_a_w2 + gla_a_b).astype(jnp.float32)) / GLA_TAU
        gla_o = gla_chunked(_heads(gq, GLA_HEADS), _heads(gk, GLA_HEADS),
                            _heads(gv, GLA_HEADS), _heads(log_a, GLA_HEADS))
        gla_o = gla_o.astype(x.dtype).transpose(0, 2, 1, 3)

        fq_h = rms_norm(_heads(fq, FOX_HEADS), fox_q_norm_g)
        fk_h = rms_norm(_heads(fk, FOX_HEADS), fox_k_norm_g)
        log_f = jax.nn.log_sigmoid((ff + fox_f_b).astype(jnp.float32)).transpose(0, 2, 1)
        fox_o = forgetting_attention(fq_h, fk_h, _heads(fv, FOX_HEADS), log_f)
        fox_o = fox_o.astype(x.dtype).transpose(0, 2, 1, 3)

        mn = rms_norm(mem, mem_norm_g)
        mk, mv = jnp.split(mn @ w_mem_kv, 2, axis=-1)
        mk = rms_norm(mk.reshape(B, mem.shape[1], MEM_HEADS, HEAD_DIM), mem_k_norm_g)
        mv = mv.reshape(B, mem.shape[1], MEM_HEADS, HEAD_DIM)
        mq_h = rms_norm(mq.reshape(B, S, MEM_HEADS, HEAD_DIM), mem_q_norm_g)
        m_logits = jnp.einsum('bshd,bmhd->bhsm', mq_h, mk).astype(jnp.float32) * HEAD_DIM ** -0.5
        m_p = jax.nn.softmax(m_logits, axis=-1)
        mem_o = jnp.einsum('bhsm,bmhd->bshd', m_p.astype(mv.dtype), mv)

        o = jnp.concatenate([gla_o, fox_o, mem_o], axis=2)
        o = rms_norm(o, out_norm_g.reshape(N_OUT_HEADS, HEAD_DIM)).reshape(B, S, -1)
        gate = jnp.concatenate([jax.nn.silu(gg), jax.nn.sigmoid(fg), jax.nn.sigmoid(mg)], axis=-1)
        h = h + (o * gate) @ w_out

        u = jax.nn.relu(rms_norm(h, mlp_norm_g) @ w_up)
        h = h + (u * u) @ w_down
    return h


N_MIXERS = 2
N_A_LAYERS = (DEPTH + N_MIXERS - 1) // N_MIXERS
N_B_LAYERS = DEPTH // N_MIXERS
HGRN_EXPAND = 128
HGRN_HEADS = D_MODEL // HGRN_EXPAND
HGRN_KEY_DIM = HGRN_HEADS * HGRN_EXPAND
HGRN_HEAD_V = D_MODEL // HGRN_HEADS
CHUNK = 64
CONV_WIDTH = 3
FFN_DIM = 5632


def rmsnorm(x, w):
    x32 = x.astype(jnp.float32)
    y = x32 * lax.rsqrt(jnp.mean(x32 * x32, axis=-1, keepdims=True) + EPS)
    return (y * w.astype(jnp.float32)).astype(x.dtype)

def dwconv3(z, w):
    L = z.shape[1]
    zp = jnp.pad(z, ((0, 0), (1, 1), (0, 0)))
    return w[0] * zp[:, :L] + w[1] * zp[:, 1:L + 1] + w[2] * zp[:, 2:]

def chunked_gated_recurrence(q, k, log_f, v):
    N, H, L, K = q.shape
    V = v.shape[-1]
    n_chunks = L // CHUNK

    def to_chunks(t):
        return t.reshape(N, H, n_chunks, CHUNK, t.shape[-1]).transpose(2, 0, 1, 3, 4)

    causal_in_chunk = jnp.tril(jnp.ones((CHUNK, CHUNK), dtype=bool))[:, :, None]

    def step(S, inp):
        qi, ki, gi, vi = inp
        b = jnp.cumsum(gi, axis=2)
        inter = jnp.einsum('nhtk,nhkv->nhtv', qi * jnp.exp(b), S)
        diff = b[:, :, :, None, :] - b[:, :, None, :, :]
        decay = jnp.exp(jnp.where(causal_in_chunk, diff, -jnp.inf))
        scores = jnp.einsum('nhtk,nhsk,nhtsk->nhts', qi, ki, decay)
        intra = jnp.einsum('nhts,nhsv->nhtv', scores, vi)
        b_last = b[:, :, -1]
        k_dec = ki * jnp.exp(b_last[:, :, None, :] - b)
        S_new = jnp.exp(b_last)[..., None] * S + jnp.einsum('nhck,nhcv->nhkv', k_dec, vi)
        return S_new, inter + intra

    S0 = jnp.zeros((N, H, K, V), jnp.float32)
    _, o = lax.scan(step, S0, (to_chunks(q), to_chunks(k), to_chunks(log_f), to_chunks(v)))
    return o.transpose(1, 2, 0, 3, 4).reshape(N, H, L, V)

def hgrn2_mixer(h, w_in, w_out, g_norm_w, lb_fwd, lb_bwd):
    B_, L, _ = h.shape
    K, D = HGRN_KEY_DIM, D_MODEL
    u = h @ w_in
    q, f_f, f_b, v, g = jnp.split(u, [K, 2 * K, 3 * K, 3 * K + D], axis=-1)
    q = jax.nn.silu(q)

    def gates(f_raw, lb):
        f = lb + (1.0 - lb) * jax.nn.sigmoid(f_raw.astype(jnp.float32))
        return 1.0 - f, jnp.log(f)

    k_f, lf_f = gates(f_f, lb_fwd)
    k_b, lf_b = gates(f_b, lb_bwd)

    def heads(t, d):
        return t.reshape(t.shape[0], L, HGRN_HEADS, d).transpose(0, 2, 1, 3).astype(jnp.float32)

    rev = lambda t: t[:, ::-1]
    qs = heads(jnp.concatenate([q, rev(q)], axis=0), HGRN_EXPAND)
    ks = heads(jnp.concatenate([k_f, rev(k_b)], axis=0), HGRN_EXPAND)
    ls = heads(jnp.concatenate([lf_f, rev(lf_b)], axis=0), HGRN_EXPAND)
    vs = heads(jnp.concatenate([v, rev(v)], axis=0), HGRN_HEAD_V)
    o = chunked_gated_recurrence(qs, ks, ls, vs)
    o = o[:B_] + o[B_:, :, ::-1]
    o = o.transpose(0, 2, 1, 3)
    gh = g.reshape(B_, L, HGRN_HEADS, HGRN_HEAD_V)
    o = rmsnorm(o, g_norm_w) * jax.nn.silu(gh.astype(jnp.float32))
    return o.reshape(B_, L, D).astype(h.dtype) @ w_out

def short_conv_mixer(h, w_in, w_conv, w_out):
    u = h @ w_in
    gate_b, gate_c, x_in = jnp.split(u, 3, axis=-1)
    z = dwconv3(gate_c * x_in, w_conv)
    return (gate_b * z) @ w_out

def conv_ffn(h, w_in, w_conv, w_out):
    up = dwconv3(h @ w_in, w_conv)
    gate, val = jnp.split(up, 2, axis=-1)
    return (jax.nn.silu(gate) * val) @ w_out

def second_inputs(seed: int = 0) -> dict:
    key = jax.random.key(seed)
    ks = jax.random.split(key, 16)
    D, K, F = D_MODEL, HGRN_KEY_DIM, FFN_DIM
    nrm = lambda k, shape, scale: jax.random.normal(k, shape, jnp.float32) * scale
    return {
        "x": nrm(ks[0], (BATCH, SEQ, D), 1.0),
        "hgrn_w_in": nrm(ks[1], (N_A_LAYERS, D, 3 * K + 2 * D), D ** -0.5),
        "hgrn_w_out": nrm(ks[2], (N_A_LAYERS, D, D), D ** -0.5),
        "hgrn_gnorm": 1.0 + nrm(ks[3], (N_A_LAYERS, HGRN_HEAD_V), 0.02),
        "hgrn_lower_bounds": nrm(ks[4], (2, N_A_LAYERS, K), 1.0),
        "sconv_w_in": nrm(ks[5], (N_B_LAYERS, D, 3 * D), D ** -0.5),
        "sconv_w_conv": nrm(ks[6], (N_B_LAYERS, CONV_WIDTH, D), CONV_WIDTH ** -0.5),
        "sconv_w_out": nrm(ks[7], (N_B_LAYERS, D, D), D ** -0.5),
        "ffn_w_in": nrm(ks[8], (DEPTH, D, 2 * F), D ** -0.5),
        "ffn_w_conv": nrm(ks[9], (DEPTH, CONV_WIDTH, 2 * F), CONV_WIDTH ** -0.5),
        "ffn_w_out": nrm(ks[10], (DEPTH, F, D), F ** -0.5),
        "norm_pre_mix": 1.0 + nrm(ks[11], (DEPTH, D), 0.02),
        "norm_post_mix": 1.0 + nrm(ks[12], (DEPTH, D), 0.02),
        "norm_pre_ffn": 1.0 + nrm(ks[13], (DEPTH, D), 0.02),
        "norm_post_ffn": 1.0 + nrm(ks[14], (DEPTH, D), 0.02),
    }

def second_block(x, hgrn_w_in, hgrn_w_out, hgrn_gnorm, hgrn_lower_bounds,
              sconv_w_in, sconv_w_conv, sconv_w_out,
              ffn_w_in, ffn_w_conv, ffn_w_out,
              norm_pre_mix, norm_post_mix, norm_pre_ffn, norm_post_ffn):
    lb = jnp.cumsum(jax.nn.softmax(hgrn_lower_bounds.astype(jnp.float32), axis=1), axis=1)
    lb = lb - lb[:, :1]
    for i in range(DEPTH):
        j = i // N_MIXERS
        h = rmsnorm(x, norm_pre_mix[i])
        if i % N_MIXERS == 0:
            m = hgrn2_mixer(h, hgrn_w_in[j], hgrn_w_out[j], hgrn_gnorm[j], lb[0, j], lb[1, j])
        else:
            m = short_conv_mixer(h, sconv_w_in[j], sconv_w_conv[j], sconv_w_out[j])
        x = x + rmsnorm(m, norm_post_mix[i])
        h = rmsnorm(x, norm_pre_ffn[i])
        x = x + rmsnorm(conv_ffn(h, ffn_w_in[i], ffn_w_conv[i], ffn_w_out[i]), norm_post_ffn[i])
    return x


def setup_inputs(seed=0):
    out = dict(first_inputs(seed))
    for name, value in second_inputs(seed + 1).items():
        if name != "x":
            out[name + "_2"] = value
    return out


def reference(
    x, mem, attn_norm_g, w_in, gla_a_w2, gla_a_b, fox_f_b, fox_q_norm_g, fox_k_norm_g,
    mem_norm_g, w_mem_kv, mem_q_norm_g, mem_k_norm_g, out_norm_g, w_out, mlp_norm_g, w_up,
    w_down, hgrn_w_in_2, hgrn_w_out_2, hgrn_gnorm_2, hgrn_lower_bounds_2, sconv_w_in_2,
    sconv_w_conv_2, sconv_w_out_2, ffn_w_in_2, ffn_w_conv_2, ffn_w_out_2, norm_pre_mix_2,
    norm_post_mix_2, norm_pre_ffn_2, norm_post_ffn_2,
):
    x = first_block(
        x, mem, attn_norm_g, w_in, gla_a_w2, gla_a_b, fox_f_b, fox_q_norm_g, fox_k_norm_g,
        mem_norm_g, w_mem_kv, mem_q_norm_g, mem_k_norm_g, out_norm_g, w_out, mlp_norm_g, w_up,
        w_down,
    )
    return second_block(
        x, hgrn_w_in_2, hgrn_w_out_2, hgrn_gnorm_2, hgrn_lower_bounds_2, sconv_w_in_2,
        sconv_w_conv_2, sconv_w_out_2, ffn_w_in_2, ffn_w_conv_2, ffn_w_out_2, norm_pre_mix_2,
        norm_post_mix_2, norm_pre_ffn_2, norm_post_ffn_2,
    )


_drawn_inputs = setup_inputs


def setup_inputs(seed=0):
    import zlib

    import numpy as np

    out = dict(_drawn_inputs(seed))
    spreads = {}
    factors = {'fox_q_norm_g': 8.0,
     'fox_k_norm_g': 8.0,
     'mem_norm_g': 6.067,
     'mem_q_norm_g': 8.0,
     'mem_k_norm_g': 8.0,
     'out_norm_g': 4.189,
     'hgrn_gnorm_2': 141.343,
     'norm_pre_mix_2': 15.488,
     'norm_post_mix_2': 29.932,
     'norm_pre_ffn_2': 4.294,
     'norm_post_ffn_2': 77.729,
     'mlp_norm_g': 3.337}
    for name, (base, spread) in spreads.items():
        noise = np.random.default_rng([zlib.crc32(name.encode()), seed]).standard_normal(out[name].shape)
        drawn = base * np.exp(spread * noise) if base else spread * noise
        out[name] = __import__('jax').numpy.asarray(drawn.astype(out[name].dtype))
    for name, factor in factors.items():
        out[name] = (out[name] * factor).astype(out[name].dtype)
    return out
```

```python
from contextlib import ExitStack

import numpy as np
import concourse.bass as bass
from concourse import mybir

F32 = mybir.dt.float32
F32R = mybir.dt.float32r
BF16 = mybir.dt.bfloat16
U8 = mybir.dt.uint8
ALU = mybir.AluOpType
ACT = mybir.ActivationFunctionType
AX = mybir.AxisListType

P = 128
T = 256
TT = T // P
D = 2048
KC = D // P
COLS = 512
UNIT = 4
WIN = 2
RAW_SLOTS = 4
SPLIT_AHEAD = 4
DFF = 4 * D
FF_BLOCKS = DFF // D
FFN = 5632
FFN_BLOCKS = FFN // COLS
HEADS4 = 4
GROUPS = D // COLS
LEVELS = 7
EPS = 1e-6
HEAD_DIM = 128
GLA_DK = 64
GLA_TAU = 16.0
NEG = -1e30

GQ, GK, GV, GG, GA, FQ, FK, FV, FG, FF, MQ, MG = (
    0, 512, 1024, 2048, 3072, 3088, 3600, 4112, 4624, 5136, 5140, 5652)

VEC = {}
_at = 0
for _name, _n in [("attn_g", KC), ("mem_g", KC), ("out_g", KC), ("mlp_g", KC), ("premix_g", KC),
                  ("preffn_g", KC), ("gla_b", 4), ("fox_b", 1), ("fq_g", 1), ("fk_g", 1), ("mq_g", 1),
                  ("mk_g", 1), ("hgrn_g", 1), ("lb", 2 * KC), ("conv", 2 * FFN // P * 3)]:
    VEC[_name] = (_at, _n)
    _at += _n
VECS = _at


class Job:

    def __init__(self, kind, act, buf, chunks=KC, first=0, needs=None):
        self.kind, self.act, self.buf = kind, act, buf
        self.chunks, self.first, self.needs = chunks, first, needs
        self.windows = chunks // WIN


class Phase:

    def __init__(self, jobs, stages, count=1, before=()):
        self.jobs, self.stages, self.count, self.before = jobs, stages, count, before
        self.windows = sum(j.windows for j in jobs)
        assert self.windows % (2 * RAW_SLOTS) == 0 and all(w < self.windows for w in stages)


EVENTS = {
    "norm_tokens": dict(squared=1, mean_square=1, rstd=1, normed=1),
    "turn_pair": dict(turned=1, high_made=1, low_made=1),
    "copy_job": dict(copied=1),
    "sigmoid_gate": dict(sigmoid_gated=1),
    "silu_gate": dict(gate_sigmoid=1, silu_gated=1),
    "head_norm": dict(squared=1, mean_square=1, rstd=1, head_normed=1, self_done=1),
    "head_turn": dict(head_turned=1, head_out=1),
    "split_small": dict(small_high=1, small_low=1),
    "small_product": dict(small_done=1, small_out=1),
    "decay_product": dict(decay_done=1, decay_z=1),
    "log_sigmoid": dict(ls_log=1, ls_out=1),
    "finish_decay": dict(decay_ready=1),
    "fox_cumsum": dict(cumsum_ready=1, self_done=2),
    "logits": dict(logits_done=1, row_max=1, probs=1),
    "turn_probs": dict(probs_turned=1, probs_t=1),
    "attend": dict(attended=1),
    "o_divide": dict(o_divided=1, self_done=1),
    "o_norm": dict(squared=1, mean_square=1, rstd=1, self_done=1),
    "o_gate": dict(o_ready=1, self_done=1),
    "o_turn": dict(o_turned=1, o_high=1, o_low=1),
    "gla_q": dict(copied=1),
    "gla_k": dict(copied=1, gla_ready=1),
    "gla_diagonal": dict(scored=1, diagonal=1),
    "gla_level": dict(scored=1, stepped=1, self_done=1),
    "gla_across": dict(scored=1, across=1),
    "gla_attend": dict(attended=1),
    "add_to_h": dict(h_added=1),
    "set_m": dict(m_set=1),
    "clear_m": dict(m_cleared=1),
    "add_to_m": dict(m_added=1),
    "relu_square": dict(relu=1, relu_sq=1, u_high=1, u_low=1),
    "forget": dict(f_sigmoid=1, f_ready=1),
    "hgrn_q": dict(gate_sigmoid=1, hgrn_ready=1, self_done=1),
    "hgrn_diagonal": dict(scored=1, diagonal=1),
    "hgrn_level": dict(scored=1, stepped=1, self_done=1),
    "hgrn_across": dict(scored=1, across=1),
    "hgrn_attend": dict(attended=1),
    "post_norm": dict(squared=1, mean_square=1, rstd=1, h_added=1, self_done=1),
    "conv": dict(conv_mid=1, conv_out=1, self_done=1),
    "swiglu": dict(gate_sigmoid=1, y_mul=1, y_high=1, y_low=1, self_done=1),
}
KINDS = sorted({k for e in EVENTS.values() for k in e})


def put(stages, window, *stage):
    stages.setdefault(window, []).append(stage)


def norm_and_turn(src, junk, vector, act):
    return [("norm_tokens", src, junk)] + [("turn_pair", vector, act, i, 4) for i in range(KC // 2)]


def first_phase():
    jobs = [Job("tokens", "B", 0, needs="low_made"), Job("tokens", "B", 1)]
    st = {}
    put(st, 1, "norm_tokens", "H", "M")
    for i in range(KC // 2):
        put(st, 3 + i, "turn_pair", "attn_g", "A", i, 2)
    put(st, 7, "head_norm", 0)
    put(st, 11, "head_turn", "mkT", "mk_g")
    put(st, 15, "copy_job", 1, "mv")
    put(st, 15, "split_small")
    put(st, 17, "small_product")
    put(st, 19, "decay_product")
    put(st, 20, "log_sigmoid", "decay")
    put(st, 21, "finish_decay")
    put(st, 22, "log_sigmoid", "fox")
    put(st, 24, "fox_cumsum")
    names = ["fq", "fk", "fv", "fg", "mq", "mg", "gq", "gk", "gv0", "gv1", "gg0", "gg1"]
    for n, name in enumerate(names):
        buf, end = n % 2, 16 + 8 * n + 7
        jobs.append(Job("features" if name in ("gq", "gk") else "tokens", "A", buf,
                        needs="low_made" if name == "fq" else None))
        if name in ("fq", "fk", "mq"):
            put(st, end, "head_norm", buf)
            put(st, end + 2, "head_turn", {"fq": "qTf", "fk": "kTf", "mq": "qTm"}[name], name + "_g")
        elif name in ("fv", "gv0", "gv1"):
            put(st, end, "copy_job", buf, {"fv": "vf", "gv0": "gv0", "gv1": "gv1"}[name])
        elif name in ("fg", "mg"):
            put(st, end, "sigmoid_gate", buf, name)
        elif name in ("gg0", "gg1"):
            put(st, end, "silu_gate", buf, name)
        elif name == "gq":
            put(st, end, "gla_q", buf)
        else:
            put(st, end, "gla_k", buf)
    for who, start in (("fox", 41), ("mem", 60)):
        for h in range(HEADS4):
            put(st, start + 2 * h, "logits", who, h)
            put(st, start + 2 * h + 1, "turn_probs", h)
            put(st, start + 2 * h + 2, "attend", who, h)
        end = start + 2 * HEADS4
        put(st, end, "o_divide", who)
        put(st, end, "o_norm", who)
        put(st, end + 1, "o_gate", who)
        put(st, end + 3, "o_turn", who)
    put(st, 80, "gla_diagonal")
    for level in range(LEVELS):
        put(st, 82 + 2 * level, "gla_level", level)
    put(st, 96, "gla_across")
    for half, (start, gated) in enumerate(((98, 104), (107, 112))):
        put(st, start, "gla_attend", half)
        put(st, start, "o_norm", f"gla{half}")
        put(st, gated, "o_gate", f"gla{half}")
        put(st, gated + 2, "o_turn", f"gla{half}")
    w = 112
    for first in (8, 0):
        for c in range(GROUPS):
            jobs.append(Job("tokens", "B", c % 2, chunks=8, first=first, needs="o_low" if c == 0 else None))
            w += 4
            put(st, w - 1, "add_to_h", c % 2, c)
    return Phase(jobs, st, before=norm_and_turn("M", "a01", "mem_g", "B"))


def mlp_phase():
    jobs, st, w = [], {}, 0
    for j in range(4):
        jobs.append(Job("features", "A", j % 2, needs="low_made" if j == 0 else None))
        w += 8
        put(st, w - 1, "relu_square", j % 2, j)
    for c in range(4):
        jobs.append(Job("tokens", "B", c % 2, needs="u_low" if c == 0 else None))
        w += 8
        put(st, w - 1, "add_to_h", c % 2, c)
    return Phase(jobs, st, count=FF_BLOCKS)


def finish_group(st, at, who):
    put(st, at, "o_norm", who)
    put(st, at + 1, "o_gate", who)
    put(st, at + 3, "o_turn", who)


def hgrn_phase(first):
    jobs = [Job("features", "A", 0, needs="low_made" if first else None), Job("features", "A", 1),
            Job("features", "A", 0), Job("tokens", "A", 1), Job("tokens", "A", 0)]
    st = {}
    if not first:
        put(st, 0, "hgrn_attend")
        finish_group(st, 0, "hgrn_before")
    base = 0 if first else 1
    put(st, 7, "forget", 0, 0, base)
    put(st, 15, "forget", 1, 1, base)
    put(st, 23, "hgrn_q", 0)
    put(st, 24, "hgrn_diagonal")
    for level in range(LEVELS):
        for direction in (0, 1):
            put(st, 25 + 2 * level + direction, "hgrn_level", level, direction)
    put(st, 31, "copy_job", 1, "v")
    put(st, 39, "hgrn_across")
    put(st, 39, "silu_gate", 0, "g")
    before = norm_and_turn("H", "M", "premix_g", "A") if first else ()
    return Phase(jobs, st, count=1 if first else GROUPS - 1, before=before)


def hgrn_out_phase():
    jobs, st, w = [], {}, 0
    put(st, 0, "hgrn_attend")
    finish_group(st, 0, "hgrn_last")
    for c in range(4):
        jobs.append(Job("tokens", "B", c % 2, chunks=12, needs="o_low" if c == 0 else None))
        w += 6
        put(st, w - 1, "set_m", c % 2, c)
    for c in range(4):
        jobs.append(Job("tokens", "B", c % 2, chunks=4, first=12, needs="o_low" if c == 0 else None))
        w += 2
        put(st, w - 1, "add_to_m", c % 2, c)
    return Phase(jobs, st)


def ffn_phases():
    head = Phase([Job("features", "A", 0, needs="low_made")], {7: [("conv", 0, "gate", 0)]},
                 before=[("post_norm", 0)] + norm_and_turn("H", "M", "preffn_g", "A") + [("clear_m",)])
    phases = [head]
    for count, last in ((FFN_BLOCKS - 1, False), (1, True)):
        st, jobs = {}, [Job("features", "A", 1)]
        put(st, 7, "conv", 1, "value", FFN_BLOCKS - 1 if last else 0)
        put(st, 7, "swiglu")
        w = 8
        if not last:
            jobs.append(Job("features", "A", 0))
            put(st, 15, "conv", 0, "gate", 1)
            w = 16
        for c in range(4):
            buf = c % 2 if last else (c + 1) % 2
            jobs.append(Job("tokens", "B", buf, chunks=4, needs="y_low" if c == 0 else None))
            w += 2
            put(st, w - 1, "add_to_m", buf, c)
        phases.append(Phase(jobs, st, count=count))
    return phases


def norm_phase(stages):
    return Phase([], {}, before=stages)


PLAN = [first_phase(),
        norm_phase(norm_and_turn("H", "M", "mlp_g", "A")), mlp_phase(),
        hgrn_phase(True), hgrn_phase(False), hgrn_out_phase(),
        *ffn_phases(),
        norm_phase([("post_norm", 1)])]
TOTAL_WINDOWS = sum(p.windows * p.count for p in PLAN)
H_ADDS_BEFORE_FFN = 8 + 4 * FF_BLOCKS + 1


class Counts:

    def __init__(self):
        self.n, self.turn, self.per = {}, None, {}

    def at(self, kind, ahead=0):
        here = self.n.get(kind, 0) + ahead
        if self.turn is not None:
            here = max(here, 0)
        if self.turn is not None and self.per.get(kind):
            return self.turn * self.per[kind] + here
        return here

    def add(self, kind, by=1):
        self.n[kind] = self.n.get(kind, 0) + by


def moved_by(phase):
    per = {"window": phase.windows}
    for stages in phase.stages.values():
        for name, *_ in stages:
            for kind, by in EVENTS[name].items():
                per[kind] = per.get(kind, 0) + by
    for job in phase.jobs:
        per[f"use{job.buf}"] = per.get(f"use{job.buf}", 0) + 1
    return per


def walk(engine, counts, window, stage):
    def stages(some):
        for name, *args in some:
            stage(name, *args)
            for kind, by in EVENTS[name].items():
                counts.add(kind, by)

    def turn(phase):
        w = 0
        for job in phase.jobs:
            for k in range(job.windows):
                window(job, k)
                counts.add("window")
                if k == job.windows - 1:
                    counts.add(f"use{job.buf}")
                stages(phase.stages.get(w, ()))
                w += 1

    for phase in PLAN:
        stages(phase.before)
        if phase.count == 1:
            turn(phase)
            continue
        start = dict(counts.n)
        with engine.Fori(0, phase.count) as i:
            counts.turn, counts.per = i, moved_by(phase)
            turn(phase)
            per, counts.turn, counts.per = counts.per, None, {}
        for kind, n in counts.n.items():
            assert n - start.get(kind, 0) == per.get(kind, 0), kind
            counts.n[kind] = start.get(kind, 0) + per.get(kind, 0) * phase.count


def build(nc, d, out):
    ctx = ExitStack()
    with ctx:
        def sb(name, shape, dt=F32):
            return ctx.enter_context(nc.sbuf_tensor(name, shape, dt))

        def sem(name):
            return ctx.enter_context(nc.semaphore(name))

        raw = sb("raw", [P, RAW_SLOTS, UNIT, COLS])
        w_high = sb("w_high", [P, SPLIT_AHEAD, WIN, COLS], F32R)
        w_low = sb("w_low", [P, SPLIT_AHEAD, WIN, COLS], F32R)
        act_high = {n: sb(f"act{n}_high", [P, KC, T], F32R) for n in "AB"}
        act_low = {n: sb(f"act{n}_low", [P, KC, T], F32R) for n in "AB"}
        H = sb("H", [P, TT, D])
        M = sb("M", [P, TT, D])
        slots = sb("slots", [P, 10, 1024])
        vec = sb("vec", [P, VECS])
        ident = sb("ident", [P, P])
        ident16 = sb("ident16", [P, P], BF16)
        causal16 = sb("causal16", [P, TT, T], BF16)
        sibling = sb("sibling", [P, 2 * LEVELS, 64], U8)
        half = sb("half", [P, 8])
        sums = sb("sums", [P, 8])
        msq = sb("msq", [P, 8])
        rstd = sb("rstd", [P, 8])
        neg_max = sb("neg_max", [P, TT])
        row_sum = sb("row_sum", [P, TT, HEADS4])
        lb = sb("lb", [P, 2 * KC])
        one_minus_lb = sb("one_minus_lb", [P, 2 * KC])
        gq_scaled = sb("gq_scaled", [P, 2])
        J = [ctx.enter_context(nc.psum_tensor(f"job{b}", [P, 2, COLS], F32)) for b in range(2)]
        att = ctx.enter_context(nc.psum_tensor("att", [P, 4, COLS], F32))

        Mf = M[:, :, :].rearrange("p t n -> p (t n)")
        m_slot = lambda i: Mf[:, i * 1024:(i + 1) * 1024]
        a_slot = lambda i: slots[:, i, :]
        a2 = lambda i: slots[:, i:i + 2, :].rearrange("p a n -> p (a n)")
        sibling_raw = slots[:, 7, 0:2 * LEVELS * 64].rearrange("p (l c) -> p l c", l=2 * LEVELS)
        B1 = {"mkT": a_slot(0), "mv": a_slot(1), "qTf": a_slot(4), "kTf": a_slot(5), "vf": a_slot(6),
              "fg": a_slot(7), "qTm": a_slot(8), "mg": a_slot(9), "gv0": a_slot(0), "gv1": a_slot(1),
              "gg0": a_slot(2), "gg1": a_slot(3), "v": a_slot(4), "g": a_slot(5)}
        square, normed_heads = a_slot(2), a_slot(3)
        small_raw = a2(4)
        small_high, small_low = (x["B"][:, 0:8, :].rearrange("p c t -> p (c t)") for x in (act_high, act_low))
        w2 = slots[0:32, 6, 0:512]
        ga_sb, fox_z, fox_t = slots[:, 9, 0:256], slots[:, 9, 256:512], slots[:, 9, 512:768]
        decay_z, decay_t = a_slot(7), a_slot(8)
        cum, neg_cum, ones_row = (m_slot(1)[:, i * T:(i + 1) * T] for i in range(3))
        probs = m_slot(3)[:, 0:512].rearrange("p (i j) -> p i j", i=TT)
        probsT = m_slot(3)[:, 512:1024].rearrange("p (i j c) -> p i j c", i=TT, j=TT)
        gla = {"E": m_slot(0), "KS": m_slot(1), "QP": m_slot(2), "q": a_slot(7)}
        gla_diag = a2(4)
        gla_off = a_slot(6)
        gated = m_slot(3)
        hg = {"QP": [a_slot(0), a_slot(1)], "KS": [a_slot(2), a_slot(3)], "f": [a_slot(6), a_slot(7)],
              "q": a_slot(8), "diag": a_slot(9), "sig": m_slot(0), "kk": m_slot(1), "off": m_slot(1),
              "sq": m_slot(2)}
        y_gate, y_value, y_sig, y = a_slot(0), a_slot(1), a_slot(2), a_slot(3)

        def V(name, i=0, n=1):
            at, size = VEC[name]
            return vec[:, at + i:at + i + n]

        raw_loaded = [sem(f"raw_loaded{i}") for i in range(RAW_SLOTS)]
        high_ready, low_ready, window_done = sem("high_ready"), sem("low_ready"), sem("window_done")
        job_free = [sem("job_free0"), sem("job_free1")]
        x_loaded, mem_loaded, const_loaded, small_loaded = (
            sem("x_loaded"), sem("mem_loaded"), sem("const_loaded"), sem("small_loaded"))
        post_g_loaded, stored = sem("post_g_loaded"), sem("stored")
        pool_set, consts16, lb_step, act_step = (
            sem("pool_set"), sem("consts16"), sem("lb_step"), sem("act_step"))
        lb_exp, sibling_ready = sem("lb_exp"), sem("sibling_ready")
        S = {k: sem(k) for k in KINDS}

        def wait(engine, counts, kind, ahead=1):
            value = counts.at(kind, ahead)
            if isinstance(value, int) and value <= 0:
                return
            engine.wait_ge(S[kind], value)

        def hview(ap, m):
            return ap.rearrange("p (n two m) -> p n two m", two=2, m=m)

        def o_chunks(where, n, who):
            if who == "hgrn_last":
                return where[:, (GROUPS - 1) * 4:GROUPS * 4, :]
            return where[:, bass.ds(n.turn * 4, 4), :]

        def conv_w(n, which, base, x, tap):
            at = VEC["conv"][0] + tap + 3 * (x + 4 * base) + (FFN // P * 3 if which == "value" else 0)
            if n.turn is None:
                return vec[:, at:at + 1]
            return vec[:, bass.ds(n.turn * 12 + at, 1)]

        block = ctx.enter_context(nc.Block())

        @block.sync
        def _(sp):
            sp.dma_start(M[:, :, :], d["mem"].rearrange("(t p) n -> p t n", p=P)).then_inc(mem_loaded, 16)
            for dst, src in ((vec[:, :], d["vecs"]), (ident[:, :], d["ident"]),
                             (sibling_raw, d["sibling"]),
                             (slots[:, 8, 0:512].rearrange("p (i j) -> p i j", i=TT), d["causal"])):
                sp.dma_start(dst, src).then_inc(const_loaded, 16)
            unit = [0]

            def load(w, k, c, turn=None, per=0, dyn=None):
                u = unit[0]
                unit[0] += 1
                need = WIN * (u - RAW_SLOTS) + 2
                src = w.rearrange("(k p) n -> p k n", p=P)[:, k, c]
                if turn is not None:
                    sp.wait_ge(low_ready, turn * (2 * per) + need)
                    sp.wait_ge(low_ready, need)
                elif need > 0:
                    sp.wait_ge(low_ready, need)
                sp.dma_start(raw[:, u % RAW_SLOTS, :, :], src).then_inc(raw_loaded[u % RAW_SLOTS], 16)

            def whole(w, col):
                for k in range(0, KC, UNIT):
                    load(w, slice(k, k + UNIT), slice(col, col + COLS))

            whole(d["w_mem_kv"], 0)
            sp.dma_start(H[:, :, :], d["x"].rearrange("(t p) n -> p t n", p=P)).then_inc(x_loaded, 16)
            sp.dma_start(small_raw, d["w_small"]).then_inc(small_loaded, 16)
            sp.dma_start(w2, d["w2"]).then_inc(small_loaded, 16)
            whole(d["w_mem_kv"], COLS)
            for col in (FQ, FK, FV, FG, MQ, MG, GQ, GK, GV, GV + COLS, GG, GG + COLS):
                whole(d["w_in"], col)
            for k in (8, 0):
                for c in range(4):
                    for kk in (k, k + UNIT):
                        load(d["w_out"], slice(kk, kk + UNIT), slice(c * COLS, (c + 1) * COLS))

            def loop(count, per, body):
                at = unit[0]
                with sp.Fori(0, count) as i:
                    body(i, per)
                assert unit[0] - at == per
                unit[0] = at + per * count

            def mlp(i, per):
                for c in range(4):
                    for k in range(0, KC, UNIT):
                        load(d["w_up"], slice(k, k + UNIT), bass.ds(i * D + c * COLS, COLS), i, per)
                for c in range(4):
                    for k in range(0, KC, UNIT):
                        load(d["w_down"], bass.ds(i * KC + k, UNIT), slice(c * COLS, (c + 1) * COLS), i, per)
            loop(FF_BLOCKS, 32, mlp)

            def group(i, per):
                for part in (1, 2, 0, 3, 4):
                    for k in range(0, KC, UNIT):
                        col = i * (COLS // 2) * 2 if part == 0 else i * COLS + part * D
                        load(d["hgrn_w_in"], slice(k, k + UNIT), bass.ds(col, COLS), i, per)
            loop(GROUPS, 20, group)
            for chunks in (range(0, 12, UNIT), (12,)):
                for c in range(4):
                    for k in chunks:
                        load(d["hgrn_w_out"], slice(k, k + UNIT), slice(c * COLS, (c + 1) * COLS))
            sp.wait_ge(S["o_low"], 4 + GROUPS)
            sp.dma_start(a2(6), d["post_mix_g"].partition_broadcast(P)).then_inc(post_g_loaded, 16)
            whole(d["ffn_w_in"], 0)

            def ffn(i, per):
                for k in range(0, KC, UNIT):
                    load(d["ffn_w_in"], slice(k, k + UNIT), bass.ds(i * COLS + FFN, COLS), i, per)
                for k in range(0, KC, UNIT):
                    load(d["ffn_w_in"], slice(k, k + UNIT), bass.ds(i * COLS + COLS, COLS), i, per)
                for c in range(4):
                    load(d["ffn_w_out"], bass.ds(i * UNIT, UNIT), slice(c * COLS, (c + 1) * COLS), i, per)
            loop(FFN_BLOCKS - 1, 12, ffn)
            sp.wait_ge(S["h_added"], H_ADDS_BEFORE_FFN)
            sp.dma_start(a2(6), d["post_ffn_g"].partition_broadcast(P)).then_inc(post_g_loaded, 16)
            whole(d["ffn_w_in"], FFN + (FFN_BLOCKS - 1) * COLS)
            for c in range(4):
                load(d["ffn_w_out"], slice(FFN // P - UNIT, FFN // P), slice(c * COLS, (c + 1) * COLS))
            assert 2 * unit[0] == TOTAL_WINDOWS
            sp.wait_ge(S["h_added"], H_ADDS_BEFORE_FFN + 1)
            sp.dma_start(out.rearrange("(t p) n -> p t n", p=P), H[:, :, :]).then_inc(stored, 16)
            sp.wait_ge(stored, 16)

        @block.gpsimd
        def _(pool):
            n = Counts()
            pool.memset(half[:, :], -0.5).then_inc(pool_set, 1)
            pool.wait_ge(pool_set, 1)

            def stage(name, *args):
                if name in ("norm_tokens", "head_norm", "o_norm", "post_norm"):
                    cols = 8 if name in ("head_norm", "o_norm") else TT
                    wait(pool, n, "mean_square")
                    nc.gpsimd.tensor_tensor(rstd[:, 0:cols], msq[:, 0:cols], half[:, 0:cols],
                                            ALU.pow).then_inc(S["rstd"], 1)
                elif name == "clear_m":
                    wait(pool, n, "turned", 0)
                    nc.gpsimd.memset(M[:, :, :], 0.0).then_inc(S["m_cleared"], 1)
            walk(pool, n, lambda *_: None, stage)

        @block.tensor
        def _(pe):
            n = Counts()
            made, needed = [0], [0]

            def window(job, k):
                slot = n.n.get("window", 0) % SPLIT_AHEAD
                pe.wait_ge(low_ready, n.at("window", 1))
                if k == 0:
                    used = n.at(f"use{job.buf}")
                    if not isinstance(used, int) or used > 0:
                        pe.wait_ge(job_free[job.buf], used)
                if job.needs and k == 0:
                    made[0] = {"low_made": -KC // 2, "u_low": -4}.get(job.needs, 0)
                    needed[0] = n.at(job.needs, made[0] + 1 if made[0] else 0)
                if job.needs == "low_made":
                    pe.wait_ge(S["low_made"], needed[0] + k)
                elif job.needs == "u_low" and k % 2 == 0:
                    pe.wait_ge(S["u_low"], needed[0] + k // 2)
                elif job.needs and k == 0:
                    wait(pe, n, job.needs, 0)
                for cc in range(WIN):
                    c = job.first + WIN * k + cc
                    ah, al = act_high[job.act], act_low[job.act]
                    for x in range(TT if job.kind == "tokens" else 4):
                        for a, w in ((ah, w_high), (ah, w_low), (al, w_high)):
                            begins = k == 0 and cc == 0 and a is ah and w is w_high
                            ends = k == job.windows - 1 and cc == WIN - 1 and a is al
                            if job.kind == "tokens":
                                mm = nc.tensor.matmul(J[job.buf][:, x, :], a[:, c, x * P:(x + 1) * P],
                                                      w[:, slot, cc, :], start=begins, stop=ends)
                            else:
                                mm = nc.tensor.matmul(
                                    J[job.buf][:, x // 2, (x % 2) * T:(x % 2 + 1) * T],
                                    w[:, slot, cc, x * P:(x + 1) * P], a[:, c, :],
                                    start=begins and x % 2 == 0, stop=ends, skip_group_check=True)
                mm.then_inc(window_done, 1)

            def turn_pair(vector, act, i, banks):
                bank = i % banks
                if i == 0:
                    wait(pe, n, "normed", 0)
                    for kind in ("o_low", "head_out"):
                        wait(pe, n, kind, 0)
                wait(pe, n, "low_made", 1 - banks)
                for c in range(2):
                    for t in range(TT):
                        mm = nc.tensor.transpose(att[:, bank, (2 * c + t) * P:(2 * c + t + 1) * P],
                                                 M[:, t, (2 * i + c) * P:(2 * i + c + 1) * P], ident[:, :])
                mm.then_inc(S["turned"], 1)

            def head_turn(src, event_in, event_out):
                wait(pe, n, event_in, 0)
                wait(pe, n, "head_out", 0)
                for h in range(HEADS4):
                    for t in range(TT):
                        at = h * T + t * P
                        mm = nc.tensor.transpose(att[:, 2 + at // COLS, at % COLS:at % COLS + P],
                                                 src[:, t * COLS + h * P:t * COLS + (h + 1) * P], ident[:, :])
                mm.then_inc(S[event_out], 1)

            def small_product():
                wait(pe, n, "small_low", 0)
                wait(pe, n, "low_made", 0)
                for c in range(KC):
                    for w, a in ((small_high, act_high["A"]), (small_high, act_low["A"]),
                                 (small_low, act_high["A"])):
                        mm = nc.tensor.matmul(att[:, 0, 0:T], w[:, c * P:(c + 1) * P], a[:, c, :],
                                              start=c == 0 and a is act_high["A"] and w is small_high,
                                              stop=c == KC - 1 and w is small_low)
                mm.then_inc(S["small_done"], 1)

            def decay_product():
                pe.wait_ge(small_loaded, 32)
                wait(pe, n, "small_out", 0)
                for f in range(4):
                    mm = nc.tensor.matmul(att[:, f // 2, (f % 2) * T:(f % 2 + 1) * T], w2[:, f * P:(f + 1) * P],
                                          ga_sb[0:32, :], start=True, stop=True)
                mm.then_inc(S["decay_done"], 1)

            def logits(who, h):
                qT, kT = (B1["qTf"], B1["kTf"]) if who == "fox" else (B1["qTm"], B1["mkT"])
                wait(pe, n, "head_out", 0)
                wait(pe, n, "cumsum_ready", 0)
                wait(pe, n, "probs", 0)
                pe.wait_ge(consts16, 2)
                for i in range(TT):
                    o = att[:, 0, i * T:(i + 1) * T]
                    mm = nc.tensor.matmul(o, qT[:, h * T + i * P:h * T + (i + 1) * P], kT[:, h * T:(h + 1) * T],
                                          start=True, stop=who == "mem")
                    if who == "fox":
                        row = slice(32 * h, 32 * h + 1)
                        nc.tensor.matmul(o, cum[row, i * P:(i + 1) * P], ones_row[row, :], start=False, stop=False)
                        nc.tensor.matmul(o, ones_row[row, 0:P], neg_cum[row, :], start=False, stop=False)
                        mm = nc.tensor.matmul(o, ident16[:, :], causal16[:, i, :], start=False, stop=True)
                mm.then_inc(S["logits_done"], 1)

            def turn_probs(h):
                wait(pe, n, "probs", 0)
                wait(pe, n, "probs_t", 0)
                for i in range(TT):
                    for j in range(TT):
                        mm = nc.tensor.transpose(att[:, 1, (2 * i + j) * P:(2 * i + j + 1) * P],
                                                 probs[:, i, j * P:(j + 1) * P], ident[:, :])
                mm.then_inc(S["probs_turned"], 1)

            def attend(who, h):
                v = B1["vf" if who == "fox" else "mv"]
                wait(pe, n, "probs_t", 0)
                wait(pe, n, "copied", 0)
                if h == 0:
                    wait(pe, n, "head_out", 0)
                    wait(pe, n, "o_low", 0)
                for i in range(TT):
                    for j in range(TT):
                        mm = nc.tensor.matmul(att[:, 2 + i, h * P:(h + 1) * P], probsT[:, i, j, :],
                                              v[:, j * COLS + h * P:j * COLS + (h + 1) * P],
                                              start=j == 0, stop=j == TT - 1)
                mm.then_inc(S["attended"], 1)

            def gla_head(x, head, tokens):
                rows = slice(GLA_DK * (head % 2), GLA_DK * (head % 2) + GLA_DK)
                at = (head // 2) * T
                return x[rows, at + tokens.start:at + tokens.stop]

            def gla_diagonal():
                wait(pe, n, "gla_ready", 0)
                wait(pe, n, "copied", 0)
                wait(pe, n, "o_low", 0)
                wait(pe, n, "probs_t", 0)
                for head in range(8):
                    for t in range(TT):
                        at = (head % 2) * 1024 + ((head // 2) * 2 + t) * P
                        tok = slice(t * P, (t + 1) * P)
                        mm = nc.tensor.matmul(att[:, at // COLS, at % COLS:at % COLS + P],
                                              gla_head(gla["KS"], head, tok), gla_head(gla["q"], head, tok),
                                              start=True, stop=True)
                mm.then_inc(S["scored"], 1)

            def gla_level(level):
                m = 1 << level
                wait(pe, n, "diagonal", 0)
                wait(pe, n, "stepped", 0)
                for head in range(8):
                    for t in range(TT):
                        at = ((head // 2) * 2 + t) * 64
                        tok = slice(t * P, (t + 1) * P)
                        mm = nc.tensor.matmul(att[:, head % 2, at:at + 64], gla_head(gla["KS"], head, tok),
                                              hview(gla_head(gla["QP"], head, tok), m)[:, :, 1, :],
                                              start=True, stop=True)
                mm.then_inc(S["scored"], 1)

            def gla_across():
                wait(pe, n, "stepped", 0)
                for head in range(8):
                    at = (head // 2) * P
                    mm = nc.tensor.matmul(att[:, head % 2, at:at + P], gla_head(gla["KS"], head, slice(0, P)),
                                          gla_head(gla["QP"], head, slice(P, T)), start=True, stop=True)
                mm.then_inc(S["scored"], 1)

            def gla_attend(half_):
                wait(pe, n, "across", 0)
                wait(pe, n, "copied", 0)
                wait(pe, n, "stepped", 0)
                wait(pe, n, "o_low", 0)
                v = B1[f"gv{half_}"]
                for i in range(TT):
                    for hh in range(HEADS4):
                        head = 4 * half_ + hh
                        at = (head % 2) * 1024 + ((head // 2) * 2 + i) * P
                        o = att[:, 2 + i, hh * P:(hh + 1) * P]
                        mm = nc.tensor.matmul(o, gla_diag[:, at:at + P],
                                              v[:, i * COLS + hh * P:i * COLS + (hh + 1) * P],
                                              start=True, stop=i == 0)
                        if i == 1:
                            at = (head % 2) * COLS + (head // 2) * P
                            mm = nc.tensor.matmul(o, gla_off[:, at:at + P], v[:, hh * P:(hh + 1) * P],
                                                  start=False, stop=True)
                mm.then_inc(S["attended"], 1)

            def hgrn_diagonal():
                wait(pe, n, "hgrn_ready", 0)
                wait(pe, n, "across", 0)
                for h in range(HEADS4):
                    for t in range(TT):
                        at = (2 * h + t) * P
                        tok = slice(h * T + t * P, h * T + (t + 1) * P)
                        mm = nc.tensor.matmul(att[:, at // COLS, at % COLS:at % COLS + P], hg["kk"][:, tok],
                                              hg["q"][:, tok], start=True, stop=True)
                mm.then_inc(S["scored"], 1)

            def hgrn_level(level, direction):
                m = 1 << level
                wait(pe, n, "diagonal", 0)
                wait(pe, n, "stepped", -1)
                for h in range(HEADS4):
                    for t in range(TT):
                        at = (2 * h + t) * 64
                        tok = slice(h * T + t * P, h * T + (t + 1) * P)
                        mm = nc.tensor.matmul(att[:, direction, at:at + 64], hg["KS"][direction][:, tok],
                                              hview(hg["QP"][direction][:, tok], m)[:, :, 1 - direction, :],
                                              start=True, stop=True)
                mm.then_inc(S["scored"], 1)

            def hgrn_across():
                wait(pe, n, "stepped", 0)
                for direction in (0, 1):
                    for h in range(HEADS4):
                        keys = slice(h * T + direction * P, h * T + (direction + 1) * P)
                        queries = slice(h * T + (1 - direction) * P, h * T + (2 - direction) * P)
                        mm = nc.tensor.matmul(att[:, direction, h * P:(h + 1) * P], hg["KS"][direction][:, keys],
                                              hg["QP"][direction][:, queries], start=True, stop=True)
                mm.then_inc(S["scored"], 1)

            def hgrn_attend():
                wait(pe, n, "across", 0)
                wait(pe, n, "copied", 0)
                wait(pe, n, "stepped", 0)
                wait(pe, n, "o_low", 0)
                v = B1["v"]
                for i in range(TT):
                    for h in range(HEADS4):
                        o = att[:, 2 + i, h * P:(h + 1) * P]
                        at = (2 * h + i) * P
                        nc.tensor.matmul(o, hg["diag"][:, at:at + P],
                                         v[:, i * COLS + h * P:i * COLS + (h + 1) * P], start=True, stop=False)
                        at, j = (1 - i) * COLS + h * P, 1 - i
                        mm = nc.tensor.matmul(o, hg["off"][:, at:at + P],
                                              v[:, j * COLS + h * P:j * COLS + (h + 1) * P],
                                              start=False, stop=True)
                mm.then_inc(S["attended"], 1)

            def stage(name, *args):
                if name == "turn_pair":
                    turn_pair(*args)
                elif name == "head_turn":
                    head_turn(normed_heads, "head_normed", "head_turned")
                elif name == "o_turn":
                    head_turn(gated, "o_ready", "o_turned")
                elif name in ("small_product", "decay_product", "logits", "turn_probs", "attend",
                              "gla_diagonal", "gla_level", "gla_across", "gla_attend", "hgrn_diagonal",
                              "hgrn_level", "hgrn_across", "hgrn_attend"):
                    {"small_product": small_product, "decay_product": decay_product, "logits": logits,
                     "turn_probs": turn_probs, "attend": attend, "gla_diagonal": gla_diagonal,
                     "gla_level": gla_level, "gla_across": gla_across, "gla_attend": gla_attend,
                     "hgrn_diagonal": hgrn_diagonal, "hgrn_level": hgrn_level,
                     "hgrn_across": hgrn_across, "hgrn_attend": hgrn_attend}[name](*args)

            pe.wait_ge(const_loaded, 64)
            walk(pe, n, window, stage)

        def split_window(engine, n, part):
            w = n.n.get("window", 0) + part
            u = w // WIN
            loads = u // RAW_SLOTS + 1
            if n.turn is not None:
                loads = n.turn * (n.per["window"] // (WIN * RAW_SLOTS)) + loads
            return w, w % SPLIT_AHEAD, u % RAW_SLOTS, (w % WIN) * WIN, loads

        @block.scalar
        def _(act):
            n = Counts()

            def split_high(ahead):
                w, slot, rslot, c, loads = split_window(act, n, ahead)
                if n.turn is None and w >= TOTAL_WINDOWS:
                    return
                act.wait_ge(raw_loaded[rslot], 16 * loads)
                if ahead == SPLIT_AHEAD:
                    act.wait_ge(window_done, n.at("window", 1))
                nc.scalar.activation(w_high[:, slot, :, :], raw[:, rslot, c:c + WIN, :], ACT.Copy)\
                    .then_inc(high_ready, 1)

            def job(buf):
                act.wait_ge(window_done, n.at("window"))
                return J[buf][:, :, :]

            as_job = lambda ap: ap.rearrange("p (a b) -> p a b", a=2)
            as_att = lambda: att[:, 2:4, :]

            def norm_tokens(src, junk, ready):
                s = H if src == "H" else M
                for t in range(TT):
                    ins = nc.scalar.activation(M[:, t, :] if junk == "M" else a2(2 * t), s[:, t, :],
                                               ACT.Square, accum_out=sums[:, t:t + 1])
                ins.then_inc(S["squared"], 1)

            act_steps = [0]

            def stage(name, *a):
                if name == "norm_tokens":
                    src, junk = a
                    if src == "M":
                        act.wait_ge(mem_loaded, 16)
                    else:
                        act.wait_ge(x_loaded, 16)
                        wait(act, n, "h_added", 0)
                        wait(act, n, "turned", 0)
                        wait(act, n, "o_turned", 0)
                    wait(act, n, "mean_square", 0)
                    norm_tokens(src, junk, None)
                elif name == "post_norm":
                    wait(act, n, "m_added", 0)
                    wait(act, n, "mean_square", 0)
                    wait(act, n, "y_low", 0)
                    norm_tokens("M", "a01", None)
                elif name == "turn_pair":
                    vector, to, i, banks = a
                    bank = i % banks
                    wait(act, n, "turned")
                    if i == 0 and n.n.get("window", 0):
                        act.wait_ge(window_done, n.at("window"))
                    for c in range(2):
                        ins = nc.scalar.activation(act_high[to][:, 2 * i + c, :],
                                                   att[:, bank, c * T:(c + 1) * T], ACT.Copy,
                                                   scale=V(vector, 2 * i + c))
                    ins.then_inc(S["high_made"], 1)
                elif name == "copy_job":
                    buf, to = a
                    src = job(buf)
                    wait(act, n, "attended", 0)
                    nc.scalar.activation(as_job(B1[to]), src, ACT.Copy).then_inc(S["copied"], 1)
                    act.wait_ge(S["copied"], n.at("copied", 1))
                    act.sem_inc(job_free[buf], 1)
                elif name == "sigmoid_gate":
                    buf, to = a
                    ins = nc.scalar.activation(as_job(B1[to]), job(buf), ACT.Sigmoid)
                    ins.then_inc(S["sigmoid_gated"], 1)
                    act.wait_ge(S["sigmoid_gated"], n.at("sigmoid_gated", 1))
                    act.sem_inc(job_free[buf], 1)
                elif name == "silu_gate":
                    buf, to = a
                    wait(act, n, "hgrn_ready", 0)
                    wait(act, n, "silu_gated", 0)
                    nc.scalar.activation(as_job(hg["sig"] if to == "g" else a_slot(8)), job(buf),
                                         ACT.Sigmoid).then_inc(S["gate_sigmoid"], 1)
                elif name == "head_norm":
                    wait(act, n, "mean_square", 0)
                    nc.scalar.activation(as_job(square), job(a[0]), ACT.Square).then_inc(S["squared"], 1)
                elif name == "head_turn":
                    to, vector = a
                    wait(act, n, "head_turned")
                    g = gq_scaled[:, 0:1] if vector == "fq_g" else gq_scaled[:, 1:2] if vector == "mq_g" else V(vector)
                    act.wait_ge(lb_step, 7)
                    nc.scalar.activation(as_job(B1[to]), as_att(), ACT.Copy, scale=g).then_inc(S["head_out"], 1)
                elif name == "split_small":
                    act.wait_ge(small_loaded, 32)
                    wait(act, n, "turned", 0)
                    nc.scalar.activation(small_high, small_raw, ACT.Copy).then_inc(S["small_high"], 1)
                elif name == "small_product":
                    wait(act, n, "small_done")
                    nc.scalar.activation(ga_sb, att[:, 0, 0:T], ACT.Copy)
                    nc.scalar.activation(fox_z, att[:, 0, 0:T], ACT.Identity, bias=V("fox_b"))\
                        .then_inc(S["small_out"], 1)
                elif name == "log_sigmoid":
                    z, t = (decay_z, decay_t) if a[0] == "decay" else (fox_z, fox_t)
                    wait(act, n, "decay_z", 0)
                    nc.scalar.activation(t, z, ACT.Abs).then_inc(act_step, 1)
                    act.wait_ge(act_step, act_steps[0] + 1)
                    nc.scalar.activation(t, t, ACT.Exp, scale=-1.0).then_inc(act_step, 1)
                    act.wait_ge(act_step, act_steps[0] + 2)
                    nc.scalar.activation(t, t, ACT.Ln, bias=1.0).then_inc(S["ls_log"], 1)
                    act_steps[0] += 2
                elif name == "finish_decay":
                    wait(act, n, "ls_out", 0)
                    nc.scalar.activation(gla["E"], decay_z, ACT.Exp, scale=1.0 / GLA_TAU)\
                        .then_inc(S["decay_ready"], 1)
                elif name == "logits":
                    wait(act, n, "row_max")
                    wait(act, n, "probs_turned", 0)
                    wait(act, n, "o_turned", 0)
                    h = a[1]
                    for i in range(TT):
                        ins = nc.scalar.activation(probs[:, i, :], att[:, 0, i * T:(i + 1) * T], ACT.Exp,
                                                   bias=neg_max[:, i:i + 1], accum_out=row_sum[:, i, h:h + 1])
                    ins.then_inc(S["probs"], 1)
                elif name == "o_norm":
                    who = a[0]
                    wait(act, n, "mean_square", 0)
                    if who in ("fox", "mem"):
                        wait(act, n, "o_divided", 0)
                        nc.scalar.activation(square, gated, ACT.Square).then_inc(S["squared"], 1)
                    else:
                        wait(act, n, "attended", 0)
                        nc.scalar.activation(as_job(a_slot(9) if who.startswith("gla") else hg["sq"]), as_att(),
                                             ACT.Square).then_inc(S["squared"], 1)
                elif name == "o_turn":
                    who = a[0]
                    wait(act, n, "o_turned")
                    o = att[:, 2:4, :].rearrange("p a (b t) -> p (a b) t", t=T)
                    if who.startswith("hgrn"):
                        ins = nc.scalar.activation(o_chunks(act_high["B"], n, who), o, ACT.Copy, scale=V("hgrn_g"))
                    else:
                        first = {"gla0": 0, "gla1": 4, "fox": 8, "mem": 12}[who]
                        for h in range(HEADS4):
                            ins = nc.scalar.activation(act_high["B"][:, first + h, :], o[:, h, :], ACT.Copy,
                                                       scale=V("out_g", first + h))
                    ins.then_inc(S["o_high"], 1)
                elif name == "gla_q":
                    nc.scalar.activation(as_job(gla["q"]), job(a[0]), ACT.Copy, scale=GLA_DK ** -0.5)\
                        .then_inc(S["copied"], 1)
                    act.wait_ge(S["copied"], n.at("copied", 1))
                    act.sem_inc(job_free[a[0]], 1)
                elif name == "gla_k":
                    src = job(a[0])
                    wait(act, n, "logits_done", 0)
                    nc.scalar.activation(as_job(gla["KS"]), src, ACT.Copy).then_inc(S["copied"], 1)
                    act.wait_ge(S["copied"], n.at("copied", 1))
                    act.sem_inc(job_free[a[0]], 1)
                elif name == "hgrn_diagonal":
                    wait(act, n, "scored")
                    wait(act, n, "attended", 0)
                    nc.scalar.activation(as_job(hg["diag"]), att[:, 0:2, :], ACT.Copy).then_inc(S["diagonal"], 1)
                elif name in ("gla_across", "hgrn_across"):
                    wait(act, n, "scored")
                    to = gla_off if name == "gla_across" else hg["off"]
                    nc.scalar.activation(as_job(to), att[:, 0:2, :], ACT.Copy).then_inc(S["across"], 1)
                elif name == "set_m":
                    buf, c = a
                    src = job(buf)
                    wait(act, n, "o_turned", 0)
                    wait(act, n, "turned", 0)
                    nc.scalar.activation(M[:, :, c * COLS:(c + 1) * COLS], src, ACT.Copy).then_inc(S["m_set"], 1)
                    act.wait_ge(S["m_set"], n.at("m_set", 1))
                    act.sem_inc(job_free[buf], 1)
                elif name == "relu_square":
                    buf, j = a
                    src = job(buf)
                    wait(act, n, "relu_sq", -1)
                    nc.scalar.activation(as_job(a_slot(j % 2)), src, ACT.Relu).then_inc(S["relu"], 1)
                    act.wait_ge(S["relu"], n.at("relu", 1))
                    act.sem_inc(job_free[buf], 1)
                    wait(act, n, "relu_sq")
                    nc.scalar.activation(act_high["B"][:, 4 * j:4 * j + 4, :],
                                         a_slot(2 + j % 2).rearrange("p (c t) -> p c t", t=T), ACT.Copy)\
                        .then_inc(S["u_high"], 1)
                elif name == "forget":
                    buf, direction, _ = a
                    src = job(buf)
                    wait(act, n, "stepped", 0)
                    wait(act, n, "scored", 0)
                    nc.scalar.activation(as_job(hg["f"][direction]), src, ACT.Sigmoid)
                    nc.scalar.activation(as_job(hg["KS"][direction]), src, ACT.Sigmoid, scale=-1.0)\
                        .then_inc(S["f_sigmoid"], 1)
                    act.wait_ge(S["f_sigmoid"], n.at("f_sigmoid", 1))
                    act.sem_inc(job_free[buf], 1)
                elif name == "hgrn_q":
                    src = job(a[0])
                    wait(act, n, "silu_gated", 0)
                    wait(act, n, "turned", 0)
                    nc.scalar.activation(as_job(hg["sig"]), src, ACT.Sigmoid).then_inc(S["gate_sigmoid"], 1)
                elif name == "conv":
                    buf, which, base = a
                    job(buf)
                    wait(act, n, "y_mul", 0)
                    to = y_gate if which == "gate" else y_value
                    for x in range(4):
                        ins = nc.scalar.activation(to[:, x * T:(x + 1) * T],
                                                   J[buf][:, x // 2, (x % 2) * T:(x % 2 + 1) * T], ACT.Copy,
                                                   scale=conv_w(n, which, base, x, 1))
                    ins.then_inc(S["conv_mid"], 1)
                elif name == "swiglu":
                    wait(act, n, "conv_out", 0)
                    nc.scalar.activation(y_sig, y_gate, ACT.Sigmoid).then_inc(S["gate_sigmoid"], 1)
                    wait(act, n, "y_mul")
                    nc.scalar.activation(act_high["B"][:, 0:4, :], y.rearrange("p (c t) -> p c t", t=T), ACT.Copy)\
                        .then_inc(S["y_high"], 1)

            act.wait_ge(const_loaded, 64)
            nc.scalar.activation(ident16[:, :], ident[:, :], ACT.Copy).then_inc(consts16, 1)
            nc.scalar.activation(causal16[:, :, :], slots[:, 8, 0:512].rearrange("p (i j) -> p i j", i=TT),
                                 ACT.Copy).then_inc(consts16, 1)
            nc.scalar.activation(sibling[:, :, :], sibling_raw, ACT.Copy).then_inc(sibling_ready, 1)
            act.wait_ge(lb_step, 1)
            nc.scalar.activation(lb[:, :], lb[:, :], ACT.Exp).then_inc(lb_exp, 1)
            for w in range(SPLIT_AHEAD):
                split_high(w)
            walk(act, n, lambda *_: split_high(SPLIT_AHEAD), stage)

        @block.vector
        def _(dve):
            n = Counts()

            def split_low(ahead):
                w, slot, rslot, c, loads = split_window(dve, n, ahead)
                if n.turn is None and w >= TOTAL_WINDOWS:
                    return
                dve.wait_ge(high_ready, n.at("window", 1 + ahead))
                nc.vector.tensor_tensor(w_low[:, slot, :, :], raw[:, rslot, c:c + WIN, :],
                                        w_high[:, slot, :, :].bitcast(F32), ALU.subtract).then_inc(low_ready, 1)

            as_job = lambda ap: ap.rearrange("p (a b) -> p a b", a=2)
            heads8 = lambda ap: ap.rearrange("p (x c) -> p x c", c=P)
            as_att = lambda: att[:, 2:4, :]
            bcast8 = lambda ap: ap.unsqueeze(2).to_broadcast([P, 8, P])

            def mean_square(cols, size):
                nc.vector.tensor_scalar(msq[:, 0:cols], sums[:, 0:cols], 1.0 / size, EPS, ALU.mult, ALU.add)\
                    .then_inc(S["mean_square"], 1)

            def done(ins, nth=1):
                ins.then_inc(S["self_done"], 1)
                dve.wait_ge(S["self_done"], n.at("self_done", nth))

            gate_of = {"fox": B1["fg"], "mem": B1["mg"], "gla0": B1["gg0"], "gla1": B1["gg1"],
                       "hgrn_before": B1["g"], "hgrn_last": B1["g"]}

            def step_blocks(ap, m, side):
                return hview(ap, m)[:, :, side, :]

            def total(ap, m, side, width):
                return hview(ap, m)[:, :, side, m - 1:m].to_broadcast([P, width // (2 * m), m])

            def stage(name, *a):
                if name in ("norm_tokens", "post_norm"):
                    wait(dve, n, "squared")
                    mean_square(TT, D)
                    wait(dve, n, "rstd")
                    if name == "norm_tokens":
                        s = H if a[0] == "H" else M
                        for t in range(TT):
                            ins = nc.vector.tensor_scalar(M[:, t, :], s[:, t, :], rstd[:, t:t + 1], None, ALU.mult)
                        ins.then_inc(S["normed"], 1)
                    else:
                        dve.wait_ge(post_g_loaded, 16 * (a[0] + 1))
                        for t in range(TT):
                            ins = nc.vector.scalar_tensor_tensor(M[:, t, :], M[:, t, :], rstd[:, t:t + 1], a2(6),
                                                                 ALU.mult, ALU.mult)
                        done(ins)
                        nc.vector.tensor_tensor(H[:, :, :], H[:, :, :], M[:, :, :], ALU.add)\
                            .then_inc(S["h_added"], 1)
                elif name == "turn_pair":
                    vector, to, i, banks = a
                    bank = i % banks
                    wait(dve, n, "high_made")
                    for c in range(2):
                        ins = nc.vector.scalar_tensor_tensor(
                            act_low[to][:, 2 * i + c, :], att[:, bank, c * T:(c + 1) * T],
                            V(vector, 2 * i + c), act_high[to][:, 2 * i + c, :].bitcast(F32),
                            ALU.mult, ALU.subtract)
                    ins.then_inc(S["low_made"], 1)
                elif name == "silu_gate":
                    buf, to = a
                    wait(dve, n, "gate_sigmoid")
                    if to == "g":
                        wait(dve, n, "o_ready", 0)
                    sig = hg["sig"] if to == "g" else a_slot(8)
                    ins = nc.vector.tensor_tensor(as_job(B1[to]), J[buf][:, :, :], as_job(sig), ALU.mult)
                    ins.then_inc(S["silu_gated"], 1)
                    dve.wait_ge(S["silu_gated"], n.at("silu_gated", 1))
                    dve.sem_inc(job_free[buf], 1)
                elif name == "head_norm":
                    buf = a[0]
                    wait(dve, n, "squared")
                    done(nc.vector.tensor_reduce(sums[:, 0:8], heads8(square), AX.X, ALU.add))
                    mean_square(8, HEAD_DIM)
                    wait(dve, n, "rstd")
                    wait(dve, n, "head_turned", 0)
                    for t in range(TT):
                        r = rstd[:, 4 * t:4 * t + 4].unsqueeze(2).to_broadcast([P, 4, P])
                        ins = nc.vector.tensor_tensor(
                            normed_heads[:, t * COLS:(t + 1) * COLS].rearrange("p (x c) -> p x c", c=P),
                            J[buf][:, t, :].rearrange("p (x c) -> p x c", c=P), r, ALU.mult)
                    ins.then_inc(S["head_normed"], 1)
                    dve.wait_ge(S["head_normed"], n.at("head_normed", 1))
                    dve.sem_inc(job_free[buf], 1)
                elif name == "split_small":
                    wait(dve, n, "small_high")
                    nc.vector.tensor_tensor(small_low, small_raw, small_high.bitcast(F32),
                                            ALU.subtract).then_inc(S["small_low"], 1)
                elif name == "decay_product":
                    wait(dve, n, "decay_done")
                    for f in range(4):
                        ins = nc.vector.tensor_scalar(decay_z[:, f * T:(f + 1) * T],
                                                      att[:, f // 2, (f % 2) * T:(f % 2 + 1) * T],
                                                      V("gla_b", f), None, ALU.add)
                    ins.then_inc(S["decay_z"], 1)
                elif name == "log_sigmoid":
                    z, t = (decay_z, decay_t) if a[0] == "decay" else (fox_z, fox_t)
                    wait(dve, n, "ls_log")
                    nc.vector.scalar_tensor_tensor(z, z, 0.0, t, ALU.min, ALU.subtract).then_inc(S["ls_out"], 1)
                elif name == "fox_cumsum":
                    wait(dve, n, "ls_out", 0)
                    wait(dve, n, "small_done", 0)
                    done(nc.vector.memset(ones_row, 1.0))
                    done(nc.vector.tensor_tensor_scan(cum, ones_row, fox_z, 0.0, ALU.mult, ALU.add), 2)
                    nc.vector.tensor_scalar(neg_cum, cum, -1.0, None, ALU.mult).then_inc(S["cumsum_ready"], 1)
                elif name == "logits":
                    wait(dve, n, "logits_done")
                    wait(dve, n, "probs", 0)
                    nc.vector.tensor_reduce(neg_max[:, :], att[:, 0, :].rearrange("p (i j) -> p i j", i=TT),
                                            AX.X, ALU.max, negate=True).then_inc(S["row_max"], 1)
                elif name == "turn_probs":
                    wait(dve, n, "probs_turned")
                    wait(dve, n, "attended", 0)
                    nc.vector.tensor_copy(probsT.rearrange("p i j c -> p (i j c)"), att[:, 1, :])\
                        .then_inc(S["probs_t"], 1)
                elif name == "o_divide":
                    wait(dve, n, "attended", 0)
                    wait(dve, n, "o_turned", 0)
                    rs = row_sum[:, :, :].rearrange("p i h -> p (i h)")
                    done(nc.vector.reciprocal(rs, rs))
                    for t in range(TT):
                        ins = nc.vector.tensor_tensor(
                            heads8(gated)[:, 4 * t:4 * t + 4, :],
                            att[:, 2 + t, :].rearrange("p (x c) -> p x c", c=P),
                            row_sum[:, t, :].unsqueeze(2).to_broadcast([P, 4, P]), ALU.mult)
                    ins.then_inc(S["o_divided"], 1)
                elif name == "o_norm":
                    who = a[0]
                    sq = square if who in ("fox", "mem") else a_slot(9) if who.startswith("gla") else hg["sq"]
                    wait(dve, n, "squared")
                    done(nc.vector.tensor_reduce(sums[:, 0:8], heads8(sq), AX.X, ALU.add))
                    mean_square(8, HEAD_DIM)
                elif name == "o_gate":
                    who = a[0]
                    wait(dve, n, "rstd", 0)
                    wait(dve, n, "o_turned", 0)
                    if who in ("fox", "mem"):
                        wait(dve, n, "sigmoid_gated", 0)
                        r = bcast8(rstd[:, 0:8])
                        done(nc.vector.tensor_tensor(heads8(gated), heads8(gated), r, ALU.mult))
                    else:
                        wait(dve, n, "silu_gated", 0)
                        for t in range(TT):
                            r = rstd[:, 4 * t:4 * t + 4].unsqueeze(2).to_broadcast([P, 4, P])
                            ins = nc.vector.tensor_tensor(
                                heads8(gated)[:, 4 * t:4 * t + 4, :],
                                att[:, 2 + t, :].rearrange("p (x c) -> p x c", c=P), r, ALU.mult)
                        done(ins)
                    nc.vector.tensor_tensor(gated, gated, gate_of[who], ALU.mult).then_inc(S["o_ready"], 1)
                elif name == "o_turn":
                    who = a[0]
                    wait(dve, n, "o_high")
                    o = att[:, 2:4, :].rearrange("p a (b t) -> p (a b) t", t=T)
                    if who.startswith("hgrn"):
                        ins = nc.vector.scalar_tensor_tensor(
                            o_chunks(act_low["B"], n, who), o, V("hgrn_g"),
                            o_chunks(act_high["B"], n, who).bitcast(F32), ALU.mult, ALU.subtract)
                    else:
                        first = {"gla0": 0, "gla1": 4, "fox": 8, "mem": 12}[who]
                        for h in range(HEADS4):
                            ins = nc.vector.scalar_tensor_tensor(
                                act_low["B"][:, first + h, :], o[:, h, :], V("out_g", first + h),
                                act_high["B"][:, first + h, :].bitcast(F32), ALU.mult, ALU.subtract)
                    ins.then_inc(S["o_low"], 1)
                elif name == "gla_k":
                    wait(dve, n, "copied")
                    wait(dve, n, "decay_ready", 0)
                    nc.vector.tensor_tensor(gla["QP"], gla["q"], gla["E"], ALU.mult).then_inc(S["gla_ready"], 1)
                elif name == "gla_diagonal":
                    wait(dve, n, "scored")
                    nc.vector.tensor_tensor(gla_diag.rearrange("p (x c) -> p x c", c=P),
                                            att[:, :, :].rearrange("p a (x c) -> p (a x) c", c=P),
                                            ident[:, :].unsqueeze(1).to_broadcast([P, 16, P]), ALU.mult)\
                        .then_inc(S["diagonal"], 1)
                elif name == "gla_level":
                    level, m = a[0], 1 << a[0]
                    wait(dve, n, "scored")
                    wait(dve, n, "diagonal", 0)
                    pick = sibling[:, level, :].rearrange("p (n m) -> p n m", m=m).unsqueeze(1)\
                        .to_broadcast([P, 8, 64 // m, m])
                    step(gla["QP"], gla["KS"], gla["E"], m, 0)
                    for par in range(2):
                        to = gla_diag[:, par * 1024:(par + 1) * 1024]\
                            .rearrange("p (x n two m) -> p x n two m", x=8, two=2, m=m)[:, :, :, 1, :]
                        ins = nc.vector.copy_predicated(to, pick, att[:, par, :].rearrange(
                            "p (x n m) -> p x n m", x=8, m=m))
                    ins.then_inc(S["stepped"], 1)
                    double(gla["E"], m)
                elif name == "hgrn_level":
                    level, direction = a
                    m = 1 << level
                    wait(dve, n, "scored")
                    wait(dve, n, "diagonal", 0)
                    wait(dve, n, "stepped", 0)
                    pick = sibling[:, direction * LEVELS + level, :].rearrange("p (n m) -> p n m", m=m)\
                        .unsqueeze(1).to_broadcast([P, 8, 64 // m, m])
                    step(hg["QP"][direction], hg["KS"][direction], hg["f"][direction], m, direction)
                    to = hg["diag"].rearrange("p (x n two m) -> p x n two m", x=8, two=2, m=m)
                    nc.vector.copy_predicated(to[:, :, :, 1 - direction, :], pick,
                                              att[:, direction, :].rearrange("p (x n m) -> p x n m", x=8, m=m))\
                        .then_inc(S["stepped"], 1)
                    double(hg["f"][direction], m)
                elif name == "add_to_h":
                    buf, c = a
                    dve.wait_ge(window_done, n.at("window"))
                    wait(dve, n, "h_added", 0)
                    hh = H[:, :, c * COLS:(c + 1) * COLS]
                    nc.vector.tensor_tensor(hh, J[buf][:, :, :], hh, ALU.add).then_inc(S["h_added"], 1)
                    dve.wait_ge(S["h_added"], n.at("h_added", 1))
                    dve.sem_inc(job_free[buf], 1)
                elif name == "add_to_m":
                    buf, c = a
                    dve.wait_ge(window_done, n.at("window"))
                    wait(dve, n, "m_set", 0)
                    wait(dve, n, "m_cleared", 0)
                    wait(dve, n, "m_added", 0)
                    mm = M[:, :, c * COLS:(c + 1) * COLS]
                    nc.vector.tensor_tensor(mm, J[buf][:, :, :], mm, ALU.add).then_inc(S["m_added"], 1)
                    dve.wait_ge(S["m_added"], n.at("m_added", 1))
                    dve.sem_inc(job_free[buf], 1)
                elif name == "relu_square":
                    j = a[1]
                    wait(dve, n, "relu")
                    wait(dve, n, "u_low", -1)
                    nc.vector.tensor_tensor(a_slot(2 + j % 2), a_slot(j % 2), a_slot(j % 2), ALU.mult)\
                        .then_inc(S["relu_sq"], 1)
                    wait(dve, n, "u_high")
                    nc.vector.tensor_tensor(act_low["B"][:, 4 * j:4 * j + 4, :],
                                            a_slot(2 + j % 2).rearrange("p (c t) -> p c t", t=T),
                                            act_high["B"][:, 4 * j:4 * j + 4, :].bitcast(F32), ALU.subtract)\
                        .then_inc(S["u_low"], 1)
                elif name == "forget":
                    buf, direction, base = a
                    f, k = hg["f"][direction], hg["KS"][direction]
                    wait(dve, n, "f_sigmoid")
                    for h in range(HEADS4):
                        at = HEADS4 * base + direction * KC + h
                        g = slice(at, at + 1) if n.turn is None else bass.ds(n.turn * HEADS4 + at, 1)
                        x = slice(h * T, (h + 1) * T)
                        nc.vector.tensor_scalar(f[:, x], f[:, x], one_minus_lb[:, g], lb[:, g], ALU.mult, ALU.add)
                        ins = nc.vector.tensor_scalar(k[:, x], k[:, x], one_minus_lb[:, g], None, ALU.mult)
                    ins.then_inc(S["f_ready"], 1)
                elif name == "hgrn_q":
                    buf = a[0]
                    wait(dve, n, "gate_sigmoid")
                    done(nc.vector.tensor_tensor(as_job(hg["q"]), J[buf][:, :, :], as_job(hg["sig"]), ALU.mult))
                    dve.sem_inc(job_free[buf], 1)
                    wait(dve, n, "f_ready", 0)
                    wait(dve, n, "attended", 0)
                    nc.vector.tensor_tensor(hg["QP"][0], hg["q"], hg["f"][0], ALU.mult)
                    nc.vector.tensor_tensor(hg["QP"][1], hg["q"], hg["f"][1], ALU.mult)
                    nc.vector.tensor_tensor(hg["kk"], hg["KS"][0], hg["KS"][1], ALU.add)\
                        .then_inc(S["hgrn_ready"], 1)
                elif name == "conv":
                    buf, which, base = a
                    to = y_gate if which == "gate" else y_value
                    wait(dve, n, "conv_mid")
                    for x in range(4):
                        z = J[buf][:, x // 2, (x % 2) * T:(x % 2 + 1) * T]
                        o = to[:, x * T:(x + 1) * T]
                        ins = nc.vector.scalar_tensor_tensor(o[:, 1:T], z[:, 0:T - 1], conv_w(n, which, base, x, 0), o[:, 1:T],
                                                             ALU.mult, ALU.add)
                    done(ins)
                    for x in range(4):
                        z = J[buf][:, x // 2, (x % 2) * T:(x % 2 + 1) * T]
                        o = to[:, x * T:(x + 1) * T]
                        ins = nc.vector.scalar_tensor_tensor(o[:, 0:T - 1], z[:, 1:T], conv_w(n, which, base, x, 2),
                                                             o[:, 0:T - 1], ALU.mult, ALU.add)
                    ins.then_inc(S["conv_out"], 1)
                    dve.wait_ge(S["conv_out"], n.at("conv_out", 1))
                    dve.sem_inc(job_free[buf], 1)
                elif name == "swiglu":
                    wait(dve, n, "y_low", 0)
                    done(nc.vector.tensor_tensor(y, y_gate, y_value, ALU.mult))
                    wait(dve, n, "gate_sigmoid")
                    nc.vector.tensor_tensor(y, y, y_sig, ALU.mult).then_inc(S["y_mul"], 1)
                    wait(dve, n, "y_high")
                    nc.vector.tensor_tensor(act_low["B"][:, 0:4, :], y.rearrange("p (c t) -> p c t", t=T),
                                            act_high["B"][:, 0:4, :].bitcast(F32), ALU.subtract)\
                        .then_inc(S["y_low"], 1)

            def step(qp, ks, f, m, direction):
                ahead, behind = (1, 0) if direction == 0 else (0, 1)
                q = step_blocks(qp, m, ahead)
                k = step_blocks(ks, m, behind)
                nc.vector.tensor_tensor(q, q, total(f, m, behind, 1024), ALU.mult)
                nc.vector.tensor_tensor(k, k, total(f, m, ahead, 1024), ALU.mult)

            def double(f, m):
                dve.wait_ge(S["stepped"], n.at("stepped", 1))
                t = hview(f, m)
                done(nc.vector.tensor_tensor(t[:, :, 1, m - 1:m], t[:, :, 0, m - 1:m], t[:, :, 1, m - 1:m],
                                             ALU.mult))

            dve.wait_ge(const_loaded, 64)
            raw_lb = V("lb", 0, 2 * KC)
            nc.vector.tensor_tensor(lb[:, :], raw_lb, raw_lb, ALU.subtract).then_inc(lb_step, 1)
            dve.wait_ge(lb_exp, 1)
            nc.vector.reciprocal(one_minus_lb[:, :], lb[:, :]).then_inc(lb_step, 1)
            dve.wait_ge(lb_step, 2)
            nc.vector.tensor_tensor(lb[:, :], lb[:, :], one_minus_lb[:, :], ALU.mult).then_inc(lb_step, 1)
            dve.wait_ge(lb_step, 3)
            nc.vector.tensor_tensor(lb[:, :], lb[:, :], lb[:, :], ALU.subtract).then_inc(lb_step, 1)
            dve.wait_ge(lb_step, 4)
            nc.vector.tensor_scalar(one_minus_lb[:, :], lb[:, :], -1.0, 1.0, ALU.mult, ALU.add).then_inc(lb_step, 1)
            nc.vector.tensor_scalar(gq_scaled[:, 0:1], V("fq_g"), HEAD_DIM ** -0.5, None, ALU.mult).then_inc(lb_step, 1)
            nc.vector.tensor_scalar(gq_scaled[:, 1:2], V("mq_g"), HEAD_DIM ** -0.5, None, ALU.mult).then_inc(lb_step, 1)
            dve.wait_ge(sibling_ready, 1)
            for w in range(SPLIT_AHEAD):
                split_low(w)
            walk(dve, n, lambda *_: split_low(SPLIT_AHEAD), stage)


def kernel(**inputs):
    from concourse import bacc
    from concourse.bass_utils import run_bass_kernel_spmd

    a = {k: np.asarray(v) for k, v in inputs.items()}

    def columns(v):
        return v.reshape(-1, P).T

    def on_rows(v, rows, height=P):
        out = np.zeros((height,) + v.shape[1:], v.dtype)
        out[rows] = v
        return out

    conv = a["ffn_w_conv_2"][0].reshape(3, -1, P).transpose(2, 1, 0).reshape(P, -1)
    parts = {"attn_g": columns(a["attn_norm_g"]), "mem_g": columns(a["mem_norm_g"]),
             "out_g": columns(a["out_norm_g"]), "mlp_g": columns(a["mlp_norm_g"]),
             "premix_g": columns(a["norm_pre_mix_2"][0]), "preffn_g": columns(a["norm_pre_ffn_2"][0]),
             "gla_b": columns(a["gla_a_b"]), "fox_b": on_rows(a["fox_f_b"][:, None], slice(0, P, 32)),
             "fq_g": columns(a["fox_q_norm_g"]), "fk_g": columns(a["fox_k_norm_g"]),
             "mq_g": columns(a["mem_q_norm_g"]), "mk_g": columns(a["mem_k_norm_g"]),
             "hgrn_g": columns(a["hgrn_gnorm_2"][0]),
             "lb": np.concatenate([columns(a["hgrn_lower_bounds_2"][i, 0]) for i in (0, 1)], 1), "conv": conv}
    w_small = np.zeros((KC, P, P), np.float32)
    w_in = a["w_in"].reshape(KC, P, -1)
    w_small[:, :, 16:32] = w_in[:, :, GA:GA + 16]
    w_small[:, :, 0:P:32] = w_in[:, :, FF:FF + 4]
    j = np.arange(P)[:, None]
    sibling = []
    for direction in (0, 1):
        for level in range(LEVELS):
            m, c = 1 << level, np.arange(64)[None]
            i = c // m * 2 * m + (1 - direction) * m + c % m
            sibling.append(j // m == (i // m) ^ 1)
    i, jj = np.arange(T).reshape(TT, P).T[:, :, None], np.arange(T)[None, None]
    arrays = {
        "x": a["x"][0], "mem": a["mem"][0], "w_in": a["w_in"], "w_mem_kv": a["w_mem_kv"],
        "w_out": a["w_out"], "w_up": a["w_up"], "w_down": a["w_down"],
        "hgrn_w_in": a["hgrn_w_in_2"][0], "hgrn_w_out": a["hgrn_w_out_2"][0],
        "ffn_w_in": a["ffn_w_in_2"][0], "ffn_w_out": a["ffn_w_out_2"][0],
        "post_mix_g": a["norm_post_mix_2"][0], "post_ffn_g": a["norm_post_ffn_2"][0],
        "vecs": np.concatenate([parts[k] for k in VEC], 1),
        "w_small": w_small.transpose(1, 0, 2).reshape(P, KC * P),
        "w2": on_rows(a["gla_a_w2"], slice(16, 32), 32),
        "ident": np.eye(P, dtype=np.float32),
        "sibling": np.stack(sibling, 1).astype(np.float32),
        "causal": np.where(jj <= i, 0.0, NEG).astype(np.float32),
    }
    arrays = {k: np.ascontiguousarray(v) for k, v in arrays.items()}
    nc = bacc.Bacc("TRN2", target_bir_lowering=False, num_devices=1)
    d = {k: nc.dram_tensor("in_" + k, v.shape, mybir.dt.from_np(v.dtype), kind="ExternalInput").ap()
         for k, v in arrays.items()}
    out = nc.dram_tensor("out", (T, D), F32, kind="ExternalOutput").ap()
    build(nc, d, out)
    r = run_bass_kernel_spmd(nc, [{"in_" + k: v for k, v in arrays.items()}], core_ids=[0])
    return r.results[0]["out"].reshape(1, T, D)
```
